# Optimizing a Trainium2 kernel written in Bass

```python
import jax, jax.numpy as jnp
from jax import lax
import numpy as np

D_MODEL = 1024
BATCH = 1
SEQ = 2048
DEPTH = 1

ATTN_HEADS = 8
ATTN_KV_HEADS = 2
ATTN_HEAD_DIM = 64
ATTN_GROUP = ATTN_HEADS // ATTN_KV_HEADS
WINDOW = 128
ATTN_BLOCK = 128
ROT_DIM = ATTN_HEAD_DIM // 4
ROPE_THETA = 500000.0
ATTN_Q_WIDTH = ATTN_HEADS * ATTN_HEAD_DIM
ATTN_KV_WIDTH = ATTN_KV_HEADS * ATTN_HEAD_DIM

DN_HEADS = 4
DN_KEY_DIM = 128
DN_VAL_DIM = 128
DN_CONV = 4
DN_CHUNK = 64
DN_K_WIDTH = DN_HEADS * DN_KEY_DIM
DN_V_WIDTH = DN_HEADS * DN_VAL_DIM
DN_CONV_DIM = 2 * DN_K_WIDTH + DN_V_WIDTH

MIX_WIDTH = ATTN_Q_WIDTH + DN_V_WIDTH

FFN_HIDDEN = ((-(-8 * D_MODEL // 3) + 255) // 256) * 256

NORM_EPS = 1e-6

IN_SPLIT_SIZES = (ATTN_Q_WIDTH, ATTN_KV_WIDTH, ATTN_KV_WIDTH, DN_CONV_DIM,
                  DN_HEADS, DN_HEADS, DN_V_WIDTH, D_MODEL, D_MODEL)
IN_WIDTH = sum(IN_SPLIT_SIZES)

kernel_name = "hybrid_swa_sink_gdn_swiglu_adaln"

F32 = jnp.float32

def rms_norm(x, gain):
    xf = x.astype(F32)
    y = xf * lax.rsqrt(jnp.mean(xf * xf, axis=-1, keepdims=True) + NORM_EPS)
    return (y * gain.astype(F32)).astype(x.dtype)

def l2_norm(x):
    return x * lax.rsqrt(jnp.sum(x * x, axis=-1, keepdims=True) + NORM_EPS)

def modulate(h, shift, scale):
    return h * (1 + scale[:, None, :]) + shift[:, None, :]

def partial_rope(x, cos, sin):
    half = ROT_DIM // 2
    x1 = x[..., :half].astype(F32)
    x2 = x[..., half:ROT_DIM].astype(F32)
    rot = jnp.concatenate([x1 * cos - x2 * sin, x2 * cos + x1 * sin], axis=-1)
    return jnp.concatenate([rot.astype(x.dtype), x[..., ROT_DIM:]], axis=-1)

def sliding_window_attention(q, k, v, sinks):
    B, S = q.shape[0], q.shape[1]
    nb = S // ATTN_BLOCK
    qb = q.astype(F32).reshape(B, nb, ATTN_BLOCK, ATTN_KV_HEADS, ATTN_GROUP, ATTN_HEAD_DIM)

    def with_prev(t):
        tb = t.astype(F32).reshape(B, nb, ATTN_BLOCK, ATTN_KV_HEADS, ATTN_HEAD_DIM)
        prev = jnp.pad(tb, ((0, 0), (1, 0), (0, 0), (0, 0), (0, 0)))[:, :-1]
        return jnp.concatenate([prev, tb], axis=2)

    kb = with_prev(k)
    vb = with_prev(v)
    s = jnp.einsum('bnqhgd,bnkhd->bnhgqk', qb, kb) * (ATTN_HEAD_DIM ** -0.5)
    qi = jnp.arange(ATTN_BLOCK)[:, None] + ATTN_BLOCK
    kj = jnp.arange(2 * ATTN_BLOCK)[None, :]
    dist = qi - kj
    band = (dist >= 0) & (dist < WINDOW)
    key_pos = jnp.arange(nb)[:, None] * ATTN_BLOCK + kj - ATTN_BLOCK
    valid = band[None] & (key_pos >= 0)[:, None, :]
    s = jnp.where(valid[None, :, None, None], s, -jnp.inf)
    sink = sinks.astype(F32).reshape(ATTN_KV_HEADS, ATTN_GROUP)[None, None, :, :, None, None]
    m = jnp.maximum(jnp.max(s, axis=-1, keepdims=True), sink)
    p = jnp.exp(s - m)
    probs = p / (jnp.sum(p, axis=-1, keepdims=True) + jnp.exp(sink - m))
    o = jnp.einsum('bnhgqk,bnkhd->bnqhgd', probs, vb)
    return o.reshape(B, S, ATTN_Q_WIDTH)

def causal_short_conv(x, w):
    y = lax.conv_general_dilated(x, w, window_strides=(1,), padding=[(DN_CONV - 1, 0)],
                                 dimension_numbers=('NWC', 'WIO', 'NWC'),
                                 feature_group_count=x.shape[-1])
    return jax.nn.silu(y)

def gated_delta_rule(q, k, v, g, beta):
    B, S, H, dk = q.shape
    dv = v.shape[-1]
    n = S // DN_CHUNK
    C = DN_CHUNK

    def chunk(t):
        return t.reshape(B, n, C, H, -1).transpose(0, 1, 3, 2, 4)

    q = chunk(q) * (dk ** -0.5)
    k = chunk(k)
    v = chunk(v)
    g = g.reshape(B, n, C, H).transpose(0, 1, 3, 2)
    beta = beta.reshape(B, n, C, H).transpose(0, 1, 3, 2)
    gc = jnp.cumsum(g, axis=-1)
    incl = jnp.tril(jnp.ones((C, C), dtype=bool))
    strict = jnp.tril(jnp.ones((C, C), dtype=bool), -1)
    decay = jnp.exp(jnp.where(incl, gc[..., :, None] - gc[..., None, :], -jnp.inf))
    kb = k * beta[..., None]
    L = jnp.where(strict, jnp.einsum('bnhid,bnhjd->bnhij', kb, k) * decay, 0.0)
    eye = jnp.eye(C, dtype=F32)
    T = lax.linalg.triangular_solve(L + eye, jnp.broadcast_to(eye, L.shape), left_side=True,
                                    lower=True, unit_diagonal=True)
    u = jnp.einsum('bnhij,bnhjd->bnhid', T, v * beta[..., None])
    w = jnp.einsum('bnhij,bnhjd->bnhid', T, kb * jnp.exp(gc)[..., None])
    a_intra = jnp.einsum('bnhid,bnhjd->bnhij', q, k) * decay
    q_dec = q * jnp.exp(gc)[..., None]
    g_last = gc[..., -1:]
    k_dec = k * jnp.exp(g_last - gc)[..., None]
    chunk_decay = jnp.exp(g_last[..., 0])

    def step(state, xs):
        u_c, w_c, q_c, k_c, a_c, d_c = xs
        v_new = u_c - jnp.einsum('bhcd,bhde->bhce', w_c, state)
        o_c = (jnp.einsum('bhcd,bhde->bhce', q_c, state)
               + jnp.einsum('bhij,bhje->bhie', a_c, v_new))
        state = state * d_c[..., None, None] + jnp.einsum('bhcd,bhce->bhde', k_c, v_new)
        return state, o_c

    xs = (jnp.moveaxis(u, 1, 0), jnp.moveaxis(w, 1, 0), jnp.moveaxis(q_dec, 1, 0),
          jnp.moveaxis(k_dec, 1, 0), jnp.moveaxis(a_intra, 1, 0), jnp.moveaxis(chunk_decay, 1, 0))
    state0 = jnp.zeros((B, H, dk, dv), dtype=F32)
    _, o = lax.scan(step, state0, xs)
    return o.transpose(1, 0, 3, 2, 4).reshape(B, S, H, dv)

def token_mixers(h, positions, w_in, conv_w, q_norm_g, k_norm_g, sinks, a_log, dt_bias,
                 dn_norm_g, w_branch, w_out):
    B, S, _ = h.shape
    split_idx = np.cumsum(IN_SPLIT_SIZES)[:-1].tolist()
    proj = h @ w_in
    aq, ak, av, dn_qkv, dn_b, dn_a, dn_z, gate_a, gate_d = jnp.split(proj, split_idx, axis=-1)

    aq = rms_norm(aq.reshape(B, S, ATTN_HEADS, ATTN_HEAD_DIM), q_norm_g)
    ak = rms_norm(ak.reshape(B, S, ATTN_KV_HEADS, ATTN_HEAD_DIM), k_norm_g)
    av = av.reshape(B, S, ATTN_KV_HEADS, ATTN_HEAD_DIM)
    inv_freq = ROPE_THETA ** (-jnp.arange(0, ROT_DIM, 2, dtype=F32) / ROT_DIM)
    ang = positions.astype(F32)[..., None] * inv_freq
    cos = jnp.cos(ang)[:, :, None, :]
    sin = jnp.sin(ang)[:, :, None, :]
    aq = partial_rope(aq, cos, sin)
    ak = partial_rope(ak, cos, sin)
    o_attn = sliding_window_attention(aq, ak, av, sinks)

    qkv = causal_short_conv(dn_qkv, conv_w)
    dq, dk_, dv_ = jnp.split(qkv, [DN_K_WIDTH, 2 * DN_K_WIDTH], axis=-1)
    dq = l2_norm(dq.reshape(B, S, DN_HEADS, DN_KEY_DIM).astype(F32))
    dk_ = l2_norm(dk_.reshape(B, S, DN_HEADS, DN_KEY_DIM).astype(F32))
    dv_ = dv_.reshape(B, S, DN_HEADS, DN_VAL_DIM).astype(F32)
    beta = jax.nn.sigmoid(dn_b.astype(F32))
    g = -jnp.exp(a_log.astype(F32)) * jax.nn.softplus(dn_a.astype(F32) + dt_bias.astype(F32))
    o_dn = gated_delta_rule(dq, dk_, dv_, g, beta)
    o_dn = rms_norm(o_dn, dn_norm_g) * jax.nn.silu(
        dn_z.astype(F32).reshape(B, S, DN_HEADS, DN_VAL_DIM))
    o_dn = o_dn.reshape(B, S, DN_V_WIDTH)

    y_attn = o_attn.astype(h.dtype) @ w_branch[:ATTN_Q_WIDTH]
    y_dn = o_dn.astype(h.dtype) @ w_branch[ATTN_Q_WIDTH:]
    merged = jax.nn.sigmoid(gate_a) * y_attn + jax.nn.sigmoid(gate_d) * y_dn
    return merged @ w_out

def swiglu(h, w_gate_up, w_down):
    gate, up = jnp.split(h @ w_gate_up, 2, axis=-1)
    return (jax.nn.silu(gate) * up) @ w_down

def setup_inputs(seed: int = 0) -> dict:
    key = jax.random.key(seed)
    ks = jax.random.split(key, 24)
    D = D_MODEL

    def nrm(k, shape, fan_in):
        return jax.random.normal(k, shape, F32) * (fan_in ** -0.5)

    def gain(k, shape):
        return 1.0 + 0.02 * jax.random.normal(k, shape, F32)

    x = jax.random.normal(ks[0], (BATCH, SEQ, D), F32)
    c = jax.random.normal(ks[1], (BATCH, D), F32)
    offset = jax.random.randint(ks[2], (BATCH, 1), 0, 4096, dtype=jnp.int32)
    positions = offset + jnp.arange(SEQ, dtype=jnp.int32)[None, :]
    dt = jnp.exp(jax.random.uniform(ks[13], (DEPTH, DN_HEADS), F32,
                                    jnp.log(0.001), jnp.log(0.1)))
    return {
        "x": x,
        "c": c,
        "positions": positions,
        "ada_w": nrm(ks[3], (DEPTH, D, 6 * D), D),
        "ada_b": 0.01 * jax.random.normal(ks[4], (DEPTH, 6 * D), F32),
        "norm1_g": gain(ks[5], (DEPTH, D)),
        "w_in": nrm(ks[6], (DEPTH, D, IN_WIDTH), D),
        "conv_w": nrm(ks[7], (DEPTH, DN_CONV, 1, DN_CONV_DIM), DN_CONV),
        "q_norm_g": gain(ks[8], (DEPTH, ATTN_HEAD_DIM)),
        "k_norm_g": gain(ks[9], (DEPTH, ATTN_HEAD_DIM)),
        "sinks": 0.5 * jax.random.normal(ks[10], (DEPTH, ATTN_HEADS), F32),
        "a_log": jnp.log(jax.random.uniform(ks[11], (DEPTH, DN_HEADS), F32, 1.0, 16.0)),
        "dt_bias": dt + jnp.log(-jnp.expm1(-dt)),
        "dn_norm_g": gain(ks[12], (DEPTH, DN_VAL_DIM)),
        "w_branch": nrm(ks[14], (DEPTH, MIX_WIDTH, D), ATTN_Q_WIDTH),
        "w_out": nrm(ks[15], (DEPTH, D, D), D),
        "norm2_g": gain(ks[16], (DEPTH, D)),
        "w_gate_up": nrm(ks[17], (DEPTH, D, 2 * FFN_HIDDEN), D),
        "w_down": nrm(ks[18], (DEPTH, FFN_HIDDEN, D), FFN_HIDDEN),
    }

def reference(x, c, positions, ada_w, ada_b, norm1_g, w_in, conv_w, q_norm_g, k_norm_g,
              sinks, a_log, dt_bias, dn_norm_g, w_branch, w_out, norm2_g, w_gate_up, w_down):
    cond = jax.nn.silu(c)
    for l in range(DEPTH):
        mod = cond @ ada_w[l] + ada_b[l]
        shift1, scale1, gate1, shift2, scale2, gate2 = jnp.split(mod, 6, axis=-1)
        h = modulate(rms_norm(x, norm1_g[l]), shift1, scale1)
        x = x + gate1[:, None, :] * token_mixers(
            h, positions, w_in[l], conv_w[l], q_norm_g[l], k_norm_g[l], sinks[l], a_log[l],
            dt_bias[l], dn_norm_g[l], w_branch[l], w_out[l])
        h = modulate(rms_norm(x, norm2_g[l]), shift2, scale2)
        x = x + gate2[:, None, :] * swiglu(h, w_gate_up[l], w_down[l])
    return x


_drawn_inputs = setup_inputs


def setup_inputs(seed=0):
    import zlib

    import numpy as np

    out = dict(_drawn_inputs(seed))
    spreads = {}
    factors = {'ada_b': 3.852,
     'norm1_g': 6.297,
     'q_norm_g': 36.043,
     'k_norm_g': 33.046,
     'sinks': 200.0,
     'dn_norm_g': 22.564,
     'norm2_g': 15.323}
    for name, (base, spread) in spreads.items():
        noise = np.random.default_rng([zlib.crc32(name.encode()), seed]).standard_normal(out[name].shape)
        drawn = base * np.exp(spread * noise) if base else spread * noise
        out[name] = __import__('jax').numpy.asarray(drawn.astype(out[name].dtype))
    for name, factor in factors.items():
        out[name] = (out[name] * factor).astype(out[name].dtype)
    return out
```

```python
import concourse.bass as bass
from concourse import mybir
import numpy as np

P = 128
D = 1024
SEQ = 2048
HEADS, KV_HEADS, HEAD_DIM = 8, 2, 64
GROUP = HEADS // KV_HEADS
ROT = HEAD_DIM // 4
THETA = 500000.0
DN_HEADS, DN_DIM, TAPS = 4, 128, 4
FFN = 2816
EPS = 1e-6

KD = D // P
BLK = 512
NB = SEQ // BLK
NT = BLK // P
QKW = (HEADS + KV_HEADS) * HEAD_DIM
ATW = QKW + KV_HEADS * HEAD_DIM
DNT = 3 * DN_HEADS
NFT = FFN // P
FFN_GROUPS = ((0, 8), (8, 8), (16, 6))
HALO = TAPS - 1
LEVELS = (2, 4, 8, 16, 32, 64)

C_DN = ATW
C_BA = C_DN + DNT * P
C_Z = C_BA + 2 * DN_HEADS
C_GA = C_Z + DN_HEADS * DN_DIM
C_GD = C_GA + D

U_DN = 0
U_AT = U_DN + DNT
U_BA = U_AT + 2 * (ATW // 256)
U_Z = U_BA + 1
U_GATE = U_Z + 4
U_BRANCH = U_GATE + 2 * KD
U_OUT = U_BRANCH + KD
U_FFN = U_OUT + 8
U_PER = U_FFN + 2 * NFT + 8 * len(FFN_GROUPS)
RING = 3
assert U_PER % RING == 0 and U_PER == 123
UW = 1024

J_DN = 0
J_AT = J_DN + DNT
J_BA = J_AT + 2 * 3
J_Z = J_BA + 2
J_GATE = J_Z + 4
J_BRANCH = J_GATE + 2 * KD
J_OUT = J_BRANCH + 2 * KD
J_FFN = J_OUT + 8
J_PER = J_FFN + 2 * NFT + 8 * len(FFN_GROUPS)
assert J_PER % 4 == 0


def ffn_places():
    u, j, found = U_FFN, J_FFN, []
    for first, count in FFN_GROUPS:
        found.append((u, j, first, count))
        u += 2 * count + 8
        j += 2 * count + 8
    return found


def evacuators():
    who = ["A"] * J_BRANCH + ["V"] * (J_FFN - J_BRANCH)
    for _, count in FFN_GROUPS:
        who += ["A", "V"] * count + ["V"] * 8
    return who


WHO = evacuators()
A_PER, V_PER = WHO.count("A"), WHO.count("V")


def last_uses():
    found, j, halves = [], 0, 0
    kinds = ["bank"] * DNT + ["token"] * 3 + ["two banks"] + ["token"] * 2 + ["bank"] * (2 * KD)
    kinds += ["two banks"] * KD + ["token"] * 4
    for _, count in FFN_GROUPS:
        kinds += ["bank"] * (2 * count) + ["token"] * 4
    for kind in kinds:
        if kind == "token":
            halves += 1
            found.append(("half", halves))
        j += 1 if kind == "bank" else 2
        found.append(("full", j))
    assert len(found) == U_PER and j == J_PER
    return found, halves


LAST_USE, HALVES = last_uses()


class Signal:

    def __init__(self, sem, per, before=0):
        self.sem, self.per, self.before = sem, per, before

    def at(self, b, n):
        return b * self.per + (self.before + n)


def layer_program(nc, x, cond, pos, ada_w, ada_bc, ada_br, g1, g2, qkg, sinks, a_log, dt_bias, conv_w,
                  dn_g, wstream, out):
    fp32, fp32r, i8, i32 = mybir.dt.float32, mybir.dt.float32r, mybir.dt.int8, mybir.dt.int32
    ALU, ACT, AX = mybir.AluOpType, mybir.ActivationFunctionType, mybir.AxisListType

    start = -(-nc.sbuf_base // 64) * 64 if not callable(nc.sbuf_base) else -(-nc.sbuf_base() // 64) * 64
    size = {fp32: 4, fp32r: 4, i8: 1, i32: 4}
    top = [start]

    def at(name, shape, dt, offset):
        t = nc.alloc_sbuf_tensor_at(name, shape, dt, offset=offset)
        return t, offset + -(-int(np.prod(shape[1:])) * size[dt] // 32) * 32

    def sb(name, shape, dt=fp32):
        t, top[0] = at(name, shape, dt, top[0])
        return t

    w_raw = [sb(f"w_raw{s}", [P, UW]) for s in range(RING)]
    w_hi = [sb(f"w_hi{s}", [P, UW], fp32r) for s in range(RING)]
    w_lo = [sb(f"w_lo{s}", [P, UW], fp32r) for s in range(RING)]

    zone1 = top[0]
    h_hi, o = at("h_hi", [P, KD, BLK], fp32r, zone1)
    h_lo, top[0] = at("h_lo", [P, KD, BLK], fp32r, o)
    mg_hi, o = at("mg_hi", [P, KD, BLK], fp32r, zone1)
    mg_lo, o = at("mg_lo", [P, KD, BLK], fp32r, o)
    zone2 = top[0]
    gates, top[0] = at("gates", [P, 2 * KD, BLK], fp32, zone2)
    h2_hi, o = at("h2_hi", [P, KD, BLK], fp32r, zone2)
    h2_lo, o = at("h2_lo", [P, KD, BLK], fp32r, o)
    ada_buf, o = at("ada_buf", [P, 2, KD, 512], fp32, zone2)
    zone3 = top[0]
    oT, o = at("oT", [P, 8, BLK], fp32, zone3)
    proj, o = at("proj", [P, NT, ATW], fp32, o)
    qk, o = at("qk", [P, QKW], fp32, o)
    kdup, o = at("kdup", [P, KV_HEADS, 2, HEAD_DIM], fp32, o)
    hid_hi, o = at("hid_hi", [P, 8, BLK], fp32r, zone3)
    hid_lo, top[0] = at("hid_lo", [P, 8, BLK], fp32r, o)
    ada_sum, o = at("ada_sum", [P, 2, 512], fp32, zone3)
    bias_row, o = at("bias_row", [P, 2, D], fp32, o)
    zone4 = top[0]
    qkv, o = at("qkv", [P, DNT, HALO + BLK], fp32, zone4)
    oT_hi, o = at("oT_hi", [P, 8, BLK], fp32r, zone4)
    oT_lo, top[0] = at("oT_lo", [P, 8, BLK], fp32r, o)
    x1, o = at("x1", [P, NT, D], fp32, zone4)
    z_act = sb("z_act", [P, NT, DN_HEADS * DN_DIM])
    gate_row = sb("gate_row", [P, 2, D])
    zone5 = top[0]
    HW = [P, DN_HEADS, P]
    t_q, o = at("t_q", HW, fp32, zone5)
    t_kn, o = at("t_kn", HW, fp32, o)
    t_vb, _ = at("t_vb", HW, fp32, zone4 + 24736 + 2048)
    t_knT, o = at("t_knT", HW, fp32, o)
    t_qT, o = at("t_qT", HW, fp32, o)
    t_kdec, o = at("t_kdec", HW, fp32, o)
    place_nn = o
    t_N, o = at("t_N", HW, fp32, o)
    t_NT, o = at("t_NT", HW, fp32, o)
    t_A, o = at("t_A", HW, fp32, o)
    t_AT, o = at("t_AT", HW, fp32, o)
    place_d = o
    t_dec, o = at("t_dec", HW, fp32, o)
    place_t = o
    t_T, o = at("t_T", HW, fp32, o)
    t_U, o = at("t_U", HW, fp32, o)
    qT, _ = at("qT", HW, fp32, zone4 + 24736)
    sc, o = at("sc", [P, HEADS, P + 1], fp32, o)
    mix_end = o
    t_sq, _ = at("t_sq", [P, 2 * DN_HEADS, P], fp32, place_t)
    t_X, _ = at("t_X", HW, fp32, place_d)
    t_R, _ = at("t_R", HW, fp32, zone5)
    t_vn, _ = at("t_vn", HW, fp32, place_nn + 4096)
    t_o, _ = at("t_o", HW, fp32, place_nn)
    ps_, _ = at("probs", [P, HEADS, P + 1], fp32, zone5 + 4096)
    pT = [[at(f"pT{g}{k}", HW, fp32, place_nn + (2 * g + k) * 2048)[0] for k in range(2)] for g in range(2)]
    at_sq, o = at("at_sq", [P, QKW], fp32, zone5 + 24576)
    rot_c, o = at("rot_c", [P, HEADS + KV_HEADS, 2, ROT // 2], fp32, o)
    rot_s, o = at("rot_s", [P, HEADS + KV_HEADS, 2, ROT // 2], fp32, o)
    acc = [at(f"conv_acc{k}", [P, BLK], fp32, place_t + 2048 * k)[0] for k in range(2)]
    ba_sb, _ = at("ba_sb", [2 * DN_HEADS, BLK], fp32, place_d)
    prev_sc, _ = at("prev_sc", HW, fp32, zone4 + 24736 + 2048)
    xs, o = at("xs", [P, 2, D], fp32, zone5)
    nf, o = at("nf", [P, 2, D], fp32, o)
    n_scr, o = at("n_scr", [P, D], fp32, o)
    hs = []
    for k in range(2):
        t, o = at(f"h_silu{k}", [P, BLK], fp32, o)
        hs.append(t)
    hf = []
    for k in range(2):
        t, o = at(f"h_full{k}", [P, BLK], fp32, o)
        hf.append(t)
    scaled, _ = at("scaled", [P, NT, 256], fp32, zone5 + 16384)
    br_a, q = at("br_a", [P, BLK], fp32, zone5)
    br_d, q = at("br_d", [P, BLK], fp32, q)
    br_m = []
    for k in range(2):
        t, q = at(f"br_m{k}", [P, BLK], fp32, q)
        br_m.append(t)
    top[0] = max(mix_end, o)
    ident = sb("ident", [P, P])
    tri = sb("tri", [P, P])
    gtm = sb("gtm", [P, P])
    ones = sb("ones", [P, P])
    mT = [sb(f"mT{s}", [P, P], i8) for s in (1,) + LEVELS]
    mU = [sb(f"mU{s}", [P, P], i8) for s in (1,) + LEVELS]
    m_prev = sb("m_prev", [P, P], i8)
    gains = sb("gains", [P, 2, HEAD_DIM])
    cosb = sb("cosb", [P, SEQ // P, ROT // 2])
    sinb = sb("sinb", [P, SEQ // P, ROT // 2])
    taps = sb("taps", [P, DNT, TAPS])
    mod_a = sb("mod_a", [P, 2, KD])
    mod_b = sb("mod_b", [P, 2, KD])
    nrm_g = sb("nrm_g", [P, 2, KD])
    cbias = sb("cbias", [P, 6, KD])
    dng = sb("dng", [P, 1])
    halo = sb("halo", [P, DNT, HALO])
    state = sb("state", HW)
    kT = [sb(f"kT{k}", [P, KV_HEADS, P]) for k in range(2)]
    v_prev = sb("v_prev", [P, KV_HEADS * HEAD_DIM])
    neg_first = sb("neg_first", [P, 1])
    minus_half = sb("minus_half", [P, 16])
    cs = sb("cs", [P, KD])
    dtb = sb("dtb", [P, DN_HEADS])
    nea = sb("nea", [P, DN_HEADS])
    al = sb("al", [P, DN_HEADS])
    snk = sb("snk", [P, HEADS])
    TH = [P, NT, DN_HEADS]
    g_e, g_b, g_nb, g_a, g_y, g_l, g_c, g_r, g_g, g_egc, g_dl, g_ed, g_nbe = [
        sb(f"g_{n}", TH) for n in ("e", "b", "nb", "a", "y", "l", "c", "r", "g", "egc", "dl", "ed", "nbe")]
    gcs = sb("gcs", [P, 2, NT, DN_HEADS])
    a_ss, a_rs = sb("a_ss", [P, HEADS + KV_HEADS]), sb("a_rs", [P, HEADS + KV_HEADS])
    a_mx, a_sm = sb("a_mx", [P, HEADS]), sb("a_sm", [P, HEADS])
    d_ss, d_rs = sb("d_ss", [P, 2 * DN_HEADS]), sb("d_rs", [P, 2 * DN_HEADS])
    d_rq, d_qs = sb("d_rq", [P, DN_HEADS]), sb("d_qs", [P, DN_HEADS])
    o_ss, o_rs = sb("o_ss", [P, DN_HEADS]), sb("o_rs", [P, DN_HEADS])
    n_ss, n_rs = sb("n_ss", [P, 2]), sb("n_rs", [P, 2])
    NPOS = SEQ // P
    pos_i, o = at("pos_i", [P, NPOS], i32, zone5)
    pos_f, o = at("pos_f", [P, NPOS], fp32, o)
    ang, o = at("ang", [P, NPOS, ROT // 2], fp32, o)
    turn, o = at("turn", [P, NPOS, ROT // 2], fp32, o)
    ang_r, o = at("ang_r", [P, NPOS, ROT // 2], fp32, o)

    gb = nc.alloc_psum_tensor("gb", [P, 4 * 512], fp32)
    mb = nc.alloc_psum_tensor("mb", [P, 4 * 512], fp32)

    def bank(j):
        return gb[:, (j % 4) * 512:(j % 4) * 512 + 512]

    def pair(j):
        return gb[:, (j % 4) * 512:(j % 4) * 512 + 1024].rearrange("p (t n) -> p t n", t=NT)

    def m(i, heads=4):
        return mb[:, i * 512:i * 512 + heads * P].rearrange("p (h n) -> p h n", h=heads)

    def halves(g, old):
        return mb[:, g * 1024:g * 1024 + 1024].rearrange("p (b w n) -> p b w n", b=2, w=4)[:, :, 2 * old:2 * old + 2, :]

    def by_parity(ap):
        return ap.rearrange("p (a b) n -> p b a n", b=2)

    def over_heads(ap, n=4):
        return ap.unsqueeze(2).to_broadcast([P, n, P])

    def each_head(ap, n=4):
        return ap.unsqueeze(1).to_broadcast([P, n, P])

    def sig(name, per, before=0):
        return Signal(nc.alloc_semaphore(name), per, before)

    w_loaded = [sig(f"w_loaded{s}", 16 * U_PER // RING) for s in range(RING)]
    w_high = sig("w_high", U_PER)
    w_ready = sig("w_ready", U_PER, RING)
    full = sig("full", J_PER, J_PER)
    half_done = sig("half_done", HALVES, HALVES)
    a_evac = sig("a_evac", A_PER, A_PER)
    v_evac = sig("v_evac", V_PER, V_PER)
    conv_done = sig("conv_done", DNT)
    silu_done = sig("silu_done", DNT, 2)
    n_sq, n_ms, n_pow, n_xn, n_turn, n_full, n_high, n_ready = [
        sig(f"n_{s}", 8, 4) for s in ("sq", "ms", "pow", "xn", "turn", "full", "high", "ready")]
    n_scaled = sig("n_scaled", NT)
    xs_loaded = [sig(f"xs_loaded{k}", 32, 32) for k in range(2)]
    x1_loaded = sig("x1_loaded", 16)
    x1_out = sig("x1_out", 1)
    x1_done = sig("x1_done", 4)
    stored = sig("stored", 64, 64)
    ba_evac, ba_turned = sig("ba_evac", 1), sig("ba_turned", 1)
    g_exp, g_add, g_abs, g_y1, g_ln, g_ready, g_sums, g_cp, g_diff, g_all, g_nbe_ready = [
        sig(f"s_g_{s}", 1) for s in ("exp", "add", "abs", "y1", "ln", "ready", "sums", "cp", "diff", "all", "nbe")]
    at_squared, at_ssq, at_rstd, qk_ready, qk_turned, qT_ready = [
        sig(s, NT) for s in ("at_squared", "at_ssq", "at_rstd", "qk_ready", "qk_turned", "qT_ready")]
    scores, own_copied = [sig(s, 2 * NT) for s in ("scores", "own_copied")]
    maxed, exped, probs_ready = [sig(s, NT) for s in ("maxed", "exped", "probs_ready")]
    probs_turned, probsT_ready = sig("probs_turned", 2 * NT), sig("probsT_ready", 2 * NT)
    attn_out, attn_saved = sig("attn_out", NT), sig("attn_saved", NT)
    tok_turned, d_sq, d_ssq, d_rstd, kn_ready, kdec_ready, kn_turned, knT_ready, clipped, decays = [
        sig(s, NT) for s in ("tok_turned", "d_sq", "d_ssq", "d_rstd", "kn_ready", "kdec_ready", "kn_turned",
                             "knT_ready", "clipped", "decays")]
    gram, na_ready, na_turned, nT_ready = [
        sig(s, NT) for s in ("gram", "na_ready", "na_turned", "nT_ready")]
    t_merged, u_merged = sig("t_merged", NT * len(LEVELS)), sig("u_merged", NT * (len(LEVELS) + 1))
    nt_prod, x_ready, u_prod = [sig(s, NT * len(LEVELS)) for s in ("nt_prod", "x_ready", "u_prod")]
    t_prod = sig("t_prod", NT * (len(LEVELS) - 1))
    vn_prod, vn_ready, o_prod, kv_prod, s_ready = (sig("vn_prod", NT), sig("vn_ready", NT), sig("o_prod", NT),
                                                   sig("kv_prod", NT), sig("s_ready", NT, 1))
    o_sq, o_ssq, o_rstd, o_ready, o_turned, dn_saved = [
        sig(s, NT) for s in ("o_sq", "o_ssq", "o_rstd", "o_ready", "o_turned", "dn_saved")]
    oT_high, oT_ready = sig("oT_high", 2), sig("oT_ready", 2)
    gate_open, mg_full, mg_high, mg_ready = [sig(s, KD) for s in ("gate_open", "mg_full", "mg_high", "mg_ready")]
    hid_high, hid_ready = sig("hid_high", NFT), sig("hid_ready", NFT)
    consts_in, pool_set, pos_in = [nc.alloc_semaphore(s) for s in ("consts_in", "pool_set", "pos_in")]
    ada_in = [nc.alloc_semaphore(f"ada_in{k}") for k in range(2)]
    c_silu, ada_done, ada_prod, ada_read, ang_done, sin_done, nea_exp = [
        nc.alloc_semaphore(s) for s in ("c_silu", "ada_done", "ada_prod", "ada_read", "ang_done", "sin_done",
                                        "nea_exp")]
    alone = nc.alloc_semaphore("alone")
    N_CONSTS = 11

    def wait_alone(eng, signal, value):
        eng.wait_ge(signal.sem, value)
        eng.sem_inc(alone, 1)

    places = ffn_places()
    x_t = x.rearrange("(b t p) d -> b p t d", t=NT, p=P)
    out_t = out.rearrange("(b t p) d -> b p t d", t=NT, p=P)

    with nc.Block() as block:

        @block.sync
        def _(sp):
            for s in (w_ready, full, half_done, a_evac, v_evac, silu_done, stored, s_ready):
                sp.sem_inc(s.sem, s.before)
            for dst, src in ((cs, cond), (cbias, ada_bc), (nrm_g, None), (gains, qkg), (taps, conv_w), (dng, dn_g),
                             (snk, sinks), (al, a_log), (dtb, dt_bias)):
                if dst is nrm_g:
                    sp.dma_start(nrm_g[:, 0, :], g1).then_inc(consts_in, 16)
                    sp.dma_start(nrm_g[:, 1, :], g2).then_inc(consts_in, 16)
                elif dst in (snk, al, dtb):
                    sp.dma_start(dst[:, :], src.to_broadcast([P, src.shape[1]])).then_inc(consts_in, 16)
                else:
                    sp.dma_start(dst[:], src).then_inc(consts_in, 16)
            sp.dma_start(bias_row[:, :, :], ada_br.to_broadcast([P, 2 * D]).rearrange("p (a n) -> p a n", a=2)
                         ).then_inc(consts_in, 16)
            sp.dma_start(pos_i[:, :], pos).then_inc(pos_in, 16)
            for c in range(12):
                if c >= 2:
                    sp.wait_ge(ada_done, c - 1)
                sp.dma_start(ada_buf[:, c % 2], ada_w[c]).then_inc(ada_in[c % 2], 16)
                if c == 3:
                    sp.wait_ge(ang_done, 1)
                    for i in range(2):
                        sp.dma_start(xs[:, i, :], x_t[0, :, i, :]).then_inc(xs_loaded[i].sem, 16)
            for i in range(2, NT):
                sp.wait_ge(n_turn.sem, i - 1)
                sp.dma_start(xs[:, i % 2, :], x_t[0, :, i, :]).then_inc(xs_loaded[i % 2].sem, 16)

            with sp.Fori(0, NB) as b:
                for u in range(U_PER):
                    if u == U_OUT + 5:
                        sp.wait_ge(full.sem, full.at(b, J_OUT))
                        sp.dma_start(x1[:, :, :], x_t[b]).then_inc(x1_loaded.sem, 16)
                    for i in range(NT):
                        if u == U_FFN + 8 + 10 * i:
                            if i < 2:
                                sp.wait_ge(n_turn.sem, n_turn.at(b, 3 + i - 1))
                            else:
                                sp.wait_ge(n_turn.sem, n_turn.at(b, 4 + i - 1))
                            sp.dma_start(xs[:, i % 2, :], x_t[(b + 1) % NB, :, i, :]).then_inc(xs_loaded[i % 2].sem, 16)
                    sp.wait_ge(w_ready.sem, b * U_PER + (u + 1))
                    sp.dma_start(w_raw[u % RING][:, :], wstream[u]).then_inc(w_loaded[u % RING].sem, 16)
            for u in range(2):
                sp.wait_ge(w_ready.sem, NB * U_PER + u + 1)
                sp.dma_start(w_raw[u % RING][:, :], wstream[u]).then_inc(w_loaded[u % RING].sem, 16)
            sp.wait_ge(stored.sem, 64 + 64 * NB)

        @block.gpsimd
        def _(pool):
            pool.memset(tri[:, :], 1.0)
            pool.memset(gtm[:, :], 1.0)
            pool.memset(ones[:, :], 1.0)
            pool.memset(ident[:, :], 1.0)
            pool.memset(minus_half[:, :], -0.5)
            pool.memset(neg_first[:, :], -1e30)
            for t in mT + mU:
                pool.memset(t[:, :], 0)
            pool.memset(m_prev[:, :], 1)
            pool.memset(halo[:, :, :], 0.0)
            pool.memset(state[:, :, :], 0.0)
            pool.memset(v_prev[:, :], 0.0)
            pool.memset(kT[1][:, :, :], 0.0)
            pool.drain()

            def keep(ap, pattern, base, mult, op=ALU.is_ge):
                pool.affine_select(out=ap, in_=ap, compare_op=op, fill=0.0, base=base, pattern=pattern,
                                   channel_multiplier=mult)

            keep(ident[:, :], [[-1, P]], 0, 1, ALU.is_equal)
            keep(tri[:, :], [[1, P]], 0, -1)
            keep(gtm[:, :], [[-1, P]], -1, 1)
            keep(m_prev[:, :], [[1, P]], -1, -1)
            for s, t, u in zip((1,) + LEVELS, mT, mU):
                tv = t[:, :].rearrange("p (n r) -> p n r", r=2 * s)[:, :, 0:s]
                uv = u[:, :].rearrange("p (n r) -> p n r", r=2 * s)[:, :, s:2 * s]
                pool.memset(tv, 1)
                pool.memset(uv, 1)
            pool.drain()
            for s, t, u in zip((1,) + LEVELS, mT, mU):
                n = P // (2 * s)
                tv = t[:, :].rearrange("p (n r) -> p n r", r=2 * s)[:, :, 0:s]
                uv = u[:, :].rearrange("p (n r) -> p n r", r=2 * s)[:, :, s:2 * s]
                keep(tv, [[-2 * s, n], [0, s]], -s, 1)
                keep(uv, [[-2 * s, n], [0, s]], 0, 1)
            pool.drain()
            for s, t, u in zip((1,) + LEVELS, mT, mU):
                n = P // (2 * s)
                tv = t[:, :].rearrange("p (n r) -> p n r", r=2 * s)[:, :, 0:s]
                uv = u[:, :].rearrange("p (n r) -> p n r", r=2 * s)[:, :, s:2 * s]
                keep(tv, [[2 * s, n], [0, s]], 2 * s - 1, -1)
                keep(uv, [[2 * s, n], [0, s]], s - 1, -1)
            pool.drain().then_inc(pool_set, 1)

            def power(dst, src, width, ready, value, done):
                pool.wait_ge(ready.sem, value)
                pool.tensor_tensor(dst, src, minus_half[:, 0:width], ALU.pow).then_inc(done.sem, 1)

            for i in range(NT):
                power(n_rs[:, i % 2:i % 2 + 1], n_ss[:, i % 2:i % 2 + 1], 1, n_ms, i + 1, n_pow)

            with pool.Fori(0, NB) as b:
                power(a_rs[:, :], a_ss[:, :], HEADS + KV_HEADS, at_ssq, at_ssq.at(b, 1), at_rstd)
                for t in range(NT):
                    power(d_rs[:, :], d_ss[:, :], 2 * DN_HEADS, d_ssq, d_ssq.at(b, t + 1), d_rstd)
                    pool.wait_ge(kn_ready.sem, kn_ready.at(b, t + 1))
                    pool.tensor_tensor(t_kdec[:, :, :], t_kn[:, :, :], over_heads(g_ed[:, t, :]), ALU.mult
                                       ).then_inc(kdec_ready.sem, 1)
                    if t < NT - 1:
                        power(a_rs[:, :], a_ss[:, :], HEADS + KV_HEADS, at_ssq, at_ssq.at(b, t + 2), at_rstd)
                    power(o_rs[:, :], o_ss[:, :], DN_HEADS, o_ssq, o_ssq.at(b, t + 1), o_rstd)
                for i in range(NT + 1):
                    if i < NT:
                        power(n_rs[:, i % 2:i % 2 + 1], n_ss[:, i % 2:i % 2 + 1], 1, n_ms, n_ms.at(b, i + 1), n_pow)
                    if i:
                        f = nf[:, (i - 1) % 2, :].rearrange("p (k n) -> p k n", k=KD)
                        pool.wait_ge(n_scaled.sem, n_scaled.at(b, i))
                        pool.tensor_tensor(f, f, mod_b[:, 1, :].unsqueeze(2).to_broadcast([P, KD, P]), ALU.add
                                           ).then_inc(n_full.sem, 1)
                for i in range(NT, 2 * NT):
                    power(n_rs[:, i % 2:i % 2 + 1], n_ss[:, i % 2:i % 2 + 1], 1, n_ms, n_ms.at(b, i + 1), n_pow)

        @block.scalar
        def _(act):
            act.wait_ge(consts_in, 16 * N_CONSTS)
            act.activation(cs[:, :], cs[:, :], ACT.Silu).then_inc(c_silu, 1)
            act.activation(nea[:, :], al[:, :], ACT.Exp).then_inc(nea_exp, 1)
            act.wait_ge(ang_done, 1)
            act.activation(sinb[:, :, :], ang_r[:, :, :], ACT.Sin).then_inc(sin_done, 1)
            act.wait_ge(ang_done, 2)
            act.activation(cosb[:, :, :], ang[:, :, :], ACT.Sin).then_inc(sin_done, 1)

            def unit_used(b, u):
                which, n = LAST_USE[u % U_PER]
                signal = full if which == "full" else half_done
                act.wait_ge(signal.sem, signal.at(b, n + u // U_PER * signal.per))

            def split(b, u):
                s = u % RING
                act.wait_ge(w_loaded[s].sem, b * w_loaded[s].per + 16 * (u // RING + 1))
                unit_used(b, u - RING)
                act.activation(w_hi[s][:, :], w_raw[s][:, :], ACT.Copy).then_inc(w_high.sem, 1)

            def emptied(j, n=1):
                return WHO[:j].count("A") + n

            def norm_squares(n, src):
                act.activation(n_scr[:, :], src, ACT.Square, accum_out=n_ss[:, n % 2:n % 2 + 1]).then_inc(n_sq.sem, 1)

            def norm_high(n, value, hi):
                act.wait_ge(n_full.sem, value)
                t = n % NT
                act.activation(hi[:, :, t * P:t * P + P], nf[:, n % 2, :].rearrange("p (k n) -> p k n", k=KD), ACT.Copy
                               ).then_inc(n_high.sem, 1)

            def store_columns(b, c):
                part = slice(c * 256, c * 256 + 256)
                act.wait_ge(x1_done.sem, x1_done.at(b, c + 1))
                act.dma_start(out_t[b, :, :, part], x1[:, :, part]).then_inc(stored.sem, 16)

            act.wait_ge(pool_set, 1)
            for t in range(NT):
                act.wait_ge(xs_loaded[t % 2].sem, 16 * (t // 2 + 1))
                if t:
                    act.wait_ge(n_xn.sem, t)
                norm_squares(t, xs[:, t % 2, :])
                norm_high(t, t + 1, h_hi)
            split(0, 0)
            split(0, 1)
            with act.Fori(0, NB) as b:
                for c in range(DNT + 1):
                    if c < DNT:
                        split(b, U_DN + c + 2)
                        if c == 0:
                            act.wait_ge(stored.sem, stored.at(b, 0))
                        act.wait_ge(full.sem, full.at(b, J_DN + c + 1))
                        act.activation(qkv[:, c, HALO:], bank(J_DN + c), ACT.Copy).then_inc(a_evac.sem, 1)
                    if c:
                        act.wait_ge(conv_done.sem, conv_done.at(b, c))
                        act.activation(qkv[:, c - 1, HALO:], acc[(c - 1) % 2][:, :], ACT.Silu).then_inc(silu_done.sem, 1)
                for c in range(3):
                    split(b, U_AT + 2 * c + 2)
                    split(b, U_AT + 2 * c + 3)
                    j = J_AT + 2 * c
                    act.wait_ge(full.sem, full.at(b, j + 2))
                    act.activation(proj[:, :, c * 256:c * 256 + 256], pair(j), ACT.Copy).then_inc(a_evac.sem, 2)
                act.drain()
                act.activation(at_sq[:, :], proj[:, 0, 0:QKW], ACT.Square).then_inc(at_squared.sem, 1)
                split(b, U_BA + 2)
                act.wait_ge(full.sem, full.at(b, J_BA + 2))
                act.activation(ba_sb[:, :], bank(J_BA)[0:2 * DN_HEADS, :], ACT.Copy).then_inc(a_evac.sem, 2)
                for c in range(2):
                    split(b, U_Z + 2 * c + 2)
                    split(b, U_Z + 2 * c + 3)
                    j = J_Z + 2 * c
                    act.wait_ge(full.sem, full.at(b, j + 2))
                    act.activation(z_act[:, :, c * 256:c * 256 + 256], pair(j), ACT.Silu).then_inc(a_evac.sem, 2)
                ba = mb[:, 0:NT * 8].rearrange("p (t n) -> p t n", t=NT)
                act.wait_ge(g_add.sem, g_add.at(b, 1))
                act.activation(g_e[:, :, :], ba[:, :, 0:4], ACT.Exp, scale=-1.0).then_inc(g_exp.sem, 1)
                act.activation(g_l[:, :, :], g_a[:, :, :], ACT.Abs)
                act.drain()
                act.activation(g_c[:, :, :], g_l[:, :, :], ACT.Exp, scale=-1.0).then_inc(g_abs.sem, 1)
                act.wait_ge(g_y1.sem, g_y1.at(b, 1))
                act.activation(g_l[:, :, :], g_y[:, :, :], ACT.Ln).then_inc(g_ln.sem, 1)
                sums = mb[:, 512:512 + 32].rearrange("p (a t h) -> p a t h", a=2, t=NT)
                act.wait_ge(g_sums.sem, g_sums.at(b, 1))
                act.activation(gcs[:, :, :, :], sums, ACT.Copy).then_inc(g_cp.sem, 1)
                act.activation(g_egc[:, :, :], sums[:, 0], ACT.Exp)
                act.activation(g_dl[:, :, :], sums[:, 1], ACT.Exp)
                act.wait_ge(g_diff.sem, g_diff.at(b, 1))
                act.activation(g_ed[:, :, :], g_r[:, :, :], ACT.Exp).then_inc(g_all.sem, 1)

                def squares(t):
                    act.activation(at_sq[:, :], proj[:, t, 0:QKW], ACT.Square).then_inc(at_squared.sem, 1)

                def keep_qk(t):
                    act.wait_ge(qk_turned.sem, qk_turned.at(b, t + 1))
                    act.activation(qT[:, :, :], m(2), ACT.Copy)
                    act.activation(kT[t % 2][:, :, :], m(3, 2), ACT.Copy).then_inc(qT_ready.sem, 1)

                def gate_out(i):
                    act.wait_ge(full.sem, full.at(b, J_GATE + i + 1))
                    act.activation(gates[:, i, :], bank(J_GATE + i), ACT.Copy).then_inc(a_evac.sem, 1)

                for t in range(NT):
                    cols = slice(t * P, t * P + P)
                    if t == 0:
                        keep_qk(0)
                    for g in range(2):
                        act.wait_ge(scores.sem, scores.at(b, 2 * t + g + 1))
                        act.activation(by_parity(sc[:, 4 * g:4 * g + 4, 0:P]), halves(g, 0), ACT.Copy
                                       ).then_inc(own_copied.sem, 1)
                    split(b, U_GATE + 2 + 4 * t)
                    gate_out(4 * t)
                    act.wait_ge(maxed.sem, maxed.at(b, t + 1))
                    for h in range(HEADS):
                        last = act.activation(ps_[:, h, :], sc[:, h, :], ACT.Exp, bias=a_mx[:, h:h + 1],
                                              accum_out=a_sm[:, h:h + 1])
                    last.then_inc(exped.sem, 1)
                    act.wait_ge(attn_out.sem, attn_out.at(b, t + 1))
                    act.activation(oT[:, 0:4, cols], m(3), ACT.Copy).then_inc(attn_saved.sem, 1)
                    act.wait_ge(tok_turned.sem, tok_turned.at(b, t + 1))
                    act.activation(t_sq[:, 0:4, :], m(0), ACT.Square)
                    act.activation(t_sq[:, 4:8, :], m(1), ACT.Square).then_inc(d_sq.sem, 1)
                    split(b, U_GATE + 2 + 4 * t + 1)
                    gate_out(4 * t + 1)
                    act.wait_ge(kn_turned.sem, kn_turned.at(b, t + 1))
                    act.activation(t_knT[:, :, :], m(3), ACT.Copy)
                    act.activation(t_qT[:, :, :], m(0), ACT.Copy).then_inc(knT_ready.sem, 1)
                    act.wait_ge(clipped.sem, clipped.at(b, t + 1))
                    act.activation(t_dec[:, :, :], t_dec[:, :, :], ACT.Exp, scale=-1.0).then_inc(decays.sem, 1)
                    act.activation(t_T[:, :, :], each_head(ident[:, :]), ACT.Copy)
                    act.activation(t_U[:, :, :], each_head(ident[:, :]), ACT.Copy)
                    split(b, U_GATE + 2 + 4 * t + 2)
                    act.wait_ge(na_turned.sem, na_turned.at(b, t + 1))
                    act.activation(t_NT[:, :, :], m(2), ACT.Copy).then_inc(nT_ready.sem, 1)
                    if t < NT - 1:
                        squares(t + 1)
                    for i in range(len(LEVELS)):
                        n = t * len(LEVELS) + i + 1
                        act.wait_ge(nt_prod.sem, nt_prod.at(b, n))
                        act.activation(t_X[:, :, :], m(1), ACT.Copy).then_inc(x_ready.sem, 1)
                        if i == 1 and t == NT - 1:
                            act.activation(oT_hi[:, 0:4, :], oT[:, 0:4, :], ACT.Copy).then_inc(oT_high.sem, 1)
                    gate_out(4 * t + 2)
                    split(b, U_GATE + 2 + 4 * t + 3)
                    act.wait_ge(vn_prod.sem, vn_prod.at(b, t + 1))
                    act.activation(t_vn[:, :, :], m(1), ACT.Copy).then_inc(vn_ready.sem, 1)
                    act.wait_ge(o_prod.sem, o_prod.at(b, t + 1))
                    act.activation(t_T[:, :, :], m(0), ACT.Square).then_inc(o_sq.sem, 1)
                    if t < NT - 1:
                        keep_qk(t + 1)
                    gate_out(4 * t + 3)
                    act.wait_ge(o_turned.sem, o_turned.at(b, t + 1))
                    act.activation(oT[:, 4:8, cols], m(1), ACT.Copy, scale=dng[:, 0:1]).then_inc(dn_saved.sem, 1)
                act.activation(v_prev[:, :], proj[:, NT - 1, QKW:ATW], ACT.Copy)
                act.drain()
                act.activation(oT_hi[:, 4:8, :], oT[:, 4:8, :], ACT.Copy).then_inc(oT_high.sem, 1)
                for i in range(KD + 1):
                    if i < KD:
                        split(b, U_BRANCH + i + 2)
                        act.activation(gates[:, 2 * i:2 * i + 2, :], gates[:, 2 * i:2 * i + 2, :], ACT.Sigmoid
                                       ).then_inc(gate_open.sem, 1)
                    if i:
                        act.wait_ge(mg_full.sem, mg_full.at(b, i))
                        act.activation(mg_hi[:, i - 1, :], br_m[(i - 1) % 2][:, :], ACT.Copy).then_inc(mg_high.sem, 1)
                for i in range(8):
                    split(b, U_OUT + i + 2)
                act.wait_ge(x1_out.sem, x1_out.at(b, 1))
                for i in range(NT + 2):
                    if i < NT:
                        if i:
                            act.drain()
                        norm_squares(i, x1[:, i, :])
                    if 1 <= i <= NT:
                        act.wait_ge(n_pow.sem, n_pow.at(b, i))
                        act.activation(xs[:, (i - 1) % 2, :], x1[:, i - 1, :], ACT.Copy,
                                       scale=n_rs[:, (i - 1) % 2:(i - 1) % 2 + 1]).then_inc(n_xn.sem, 1)
                    if i >= 2:
                        norm_high(i - 2, n_full.at(b, i - 1), h2_hi)
                n1 = 0
                for gi, (u0, j0, f0, count) in enumerate(places):
                    for f in range(count + 1):
                        if f < count:
                            split(b, u0 + 2 * f + 2)
                            split(b, u0 + 2 * f + 3)
                            act.wait_ge(full.sem, full.at(b, j0 + 2 * f + 1))
                            act.activation(hs[f % 2][:, :], bank(j0 + 2 * f), ACT.Silu).then_inc(a_evac.sem, 1)
                        if f:
                            if f == 1 and gi:
                                act.wait_ge(full.sem, full.at(b, j0))
                            act.wait_ge(v_evac.sem, v_evac.at(b, WHO[:j0 + 2 * f].count("V")))
                            act.activation(hid_hi[:, f - 1, :], hf[(f - 1) % 2][:, :], ACT.Copy
                                           ).then_inc(hid_high.sem, 1)
                        if gi < 2 and f in (2, 6):
                            act.wait_ge(xs_loaded[n1 % 2].sem, xs_loaded[n1 % 2].at(b, 16 * (n1 // 2 + 1)))
                            norm_squares(n1, xs[:, n1 % 2, :])
                        if gi < 2 and f in (4, 8):
                            norm_high(n1, n_full.at(b, 4 + n1 + 1), h_hi)
                            n1 += 1
                    for c in range(8):
                        split(b, u0 + 2 * count + c + 2)
                        if gi == 2 and c in (3, 5, 7):
                            store_columns(b, (c - 3) // 2)
                store_columns(b, 3)

        @block.vector
        def _(dve):
            TWO_PI = 2 * np.pi
            T1, T2 = 6.25, 17.0 / 512.0
            T3 = TWO_PI - T1 - T2
            HALF = ROT // 2
            freq = (np.float32(THETA) ** (-np.arange(0, ROT, 2, dtype=np.float32) / np.float32(ROT))).astype(np.float32)
            MAGIC = float(1.5 * 2 ** 23)
            dve.wait_ge(pos_in, 16)
            dve.tensor_copy(pos_f[:, :], pos_i[:, :])
            dve.drain()
            for f in range(HALF):
                dve.tensor_scalar(ang[:, :, f], pos_f[:, :], float(freq[f]), None, ALU.mult)
            dve.drain()
            for quarter, dst in ((0.0, ang_r), (0.25, ang)):
                dve.tensor_scalar(turn[:, :, :], ang[:, :, :], 1.0 / TWO_PI, quarter, ALU.mult, ALU.add)
                dve.drain()
                dve.tensor_scalar(turn[:, :, :], turn[:, :, :], MAGIC, None, ALU.add)
                dve.drain()
                dve.tensor_scalar(turn[:, :, :], turn[:, :, :], MAGIC, None, ALU.subtract)
                dve.drain()
                src = ang
                for part in (T1, T2, T3):
                    dve.scalar_tensor_tensor(dst[:, :, :], turn[:, :, :], -part, src[:, :, :], ALU.mult, ALU.add)
                    dve.drain()
                    src = dst
                if quarter:
                    dve.tensor_scalar(dst[:, :, :], dst[:, :, :], float(np.pi / 2), None, ALU.add)
                    dve.drain()
                dve.tensor_scalar(dst[:, :, :], dst[:, :, :], 3.1415925, -3.1415925, ALU.min, ALU.max
                                  ).then_inc(ang_done, 1)
                dve.drain()
            dve.wait_ge(consts_in, 16 * N_CONSTS)
            dve.wait_ge(nea_exp, 1)
            dve.tensor_scalar(nea[:, :], nea[:, :], -1.0, None, ALU.mult)
            dve.tensor_scalar(gains[:, 0, :], gains[:, 0, :], HEAD_DIM ** -0.5, None, ALU.mult)
            dve.wait_ge(sin_done, 2)
            dve.wait_ge(c_silu, 1)

            def modulation(c):
                v, half = divmod(c, 2)
                dve.wait_ge(ada_prod, c + 1)
                ps = mb[:, (c % 2) * 512:(c % 2) * 512 + 512]
                if v in (2, 5):
                    r = 0 if v == 2 else 1
                    dve.tensor_tensor(gate_row[:, r, half * 512:half * 512 + 512], ps,
                                      bias_row[:, r, half * 512:half * 512 + 512], ALU.add).then_inc(ada_read, 1)
                else:
                    dst = (mod_b if v in (0, 3) else mod_a)[:, v // 3, half * 4:half * 4 + 4]
                    dve.tensor_tensor(dst, ps[:, 0:4], cbias[:, v, half * 4:half * 4 + 4], ALU.add).then_inc(ada_read, 1)
                if c in (3, 9):
                    dve.drain()
                    dve.tensor_scalar(mod_a[:, v // 3, :], mod_a[:, v // 3, :], 1.0, None, ALU.add)
                    dve.drain()
                    dve.tensor_tensor(mod_a[:, v // 3, :], mod_a[:, v // 3, :], nrm_g[:, v // 3, :], ALU.mult)

            for c in range(12):
                dve.wait_ge(ada_in[c % 2], 16 * (c // 2 + 1))
                if c >= 2:
                    dve.wait_ge(ada_prod, c - 1)
                for k in range(KD):
                    if k == 0:
                        last = dve.tensor_scalar(ada_sum[:, c % 2, :], ada_buf[:, c % 2, k, :], cs[:, 0:1], None, ALU.mult)
                    else:
                        dve.drain()
                        last = dve.scalar_tensor_tensor(ada_sum[:, c % 2, :], ada_buf[:, c % 2, k, :], cs[:, k:k + 1],
                                                        ada_sum[:, c % 2, :], ALU.mult, ALU.add)
                last.then_inc(ada_done, 1)
                if c:
                    modulation(c - 1)
            modulation(11)
            dve.drain()

            def split(b, u):
                s = u % RING
                dve.wait_ge(w_high.sem, b * U_PER + (u + 1))
                dve.tensor_tensor(w_lo[s][:, :], w_raw[s][:, :], w_hi[s][:, :].bitcast(fp32), ALU.subtract
                                  ).then_inc(w_ready.sem, 1)

            def norm_mean(n, value):
                dve.wait_ge(n_sq.sem, value)
                dve.tensor_scalar(n_ss[:, n % 2:n % 2 + 1], n_ss[:, n % 2:n % 2 + 1], 1.0 / D, EPS, ALU.mult, ALU.add
                                  ).then_inc(n_ms.sem, 1)

            def norm_rows(n, value, src, dst):
                dve.wait_ge(n_pow.sem, value)
                dve.tensor_scalar(dst, src, n_rs[:, n % 2:n % 2 + 1], None, ALU.mult).then_inc(n_xn.sem, 1)

            def norm_modulate(n, value, which):
                dve.wait_ge(n_turn.sem, value)
                ps = mb[:, (n % 2) * 1024:(n % 2) * 1024 + 1024].rearrange("p (k n) -> p k n", k=KD)
                f = nf[:, n % 2, :].rearrange("p (k n) -> p k n", k=KD)
                dve.tensor_tensor(f, ps, mod_a[:, which, :].unsqueeze(2).to_broadcast([P, KD, P]), ALU.mult)
                dve.drain()
                dve.tensor_tensor(f, f, mod_b[:, which, :].unsqueeze(2).to_broadcast([P, KD, P]), ALU.add
                                  ).then_inc(n_full.sem, 1)

            def norm_low(n, value, hi, lo):
                dve.wait_ge(n_high.sem, value)
                t = n % NT
                dve.tensor_tensor(lo[:, :, t * P:t * P + P], nf[:, n % 2, :].rearrange("p (k n) -> p k n", k=KD),
                                  hi[:, :, t * P:t * P + P].bitcast(fp32), ALU.subtract).then_inc(n_ready.sem, 1)

            for t in range(NT):
                norm_mean(t, t + 1)
                norm_rows(t, t + 1, xs[:, t % 2, :], xs[:, t % 2, :])
                norm_modulate(t, t + 1, 0)
                norm_low(t, t + 1, h_hi, h_lo)
            split(0, 0)
            split(0, 1)

            NH = HEADS + KV_HEADS
            q3 = qk[:, :].rearrange("p (h d) -> p h d", d=HEAD_DIM)
            rot = q3[:, :, 0:ROT].rearrange("p h (a d) -> p h a d", a=2)

            def prepare(b, t, step):
                heads = lambda a: a.rearrange("p (h d) -> p h d", d=HEAD_DIM)
                if step == 0:
                    dve.wait_ge(at_squared.sem, at_squared.at(b, t + 1))
                    dve.tensor_reduce(a_ss[:, :], heads(at_sq[:, :]), AX.X, ALU.add)
                    dve.drain()
                    dve.tensor_scalar(a_ss[:, :], a_ss[:, :], 1.0 / HEAD_DIM, EPS, ALU.mult, ALU.add
                                      ).then_inc(at_ssq.sem, 1)
                elif step == 1:
                    dve.wait_ge(at_rstd.sem, at_rstd.at(b, t + 1))
                    dve.tensor_tensor(q3, heads(proj[:, t, 0:QKW]),
                                      a_rs[:, :].unsqueeze(2).to_broadcast([P, NH, HEAD_DIM]), ALU.mult)
                elif step == 2:
                    dve.drain()
                    dve.tensor_tensor(q3[:, 0:HEADS], q3[:, 0:HEADS],
                                      gains[:, 0, :].unsqueeze(1).to_broadcast([P, HEADS, HEAD_DIM]), ALU.mult)
                    dve.tensor_tensor(q3[:, HEADS:NH], q3[:, HEADS:NH],
                                      gains[:, 1, :].unsqueeze(1).to_broadcast([P, KV_HEADS, HEAD_DIM]), ALU.mult)
                elif step == 3:
                    def spread(a):
                        row = a.rearrange("p a d -> p (a d)").unsqueeze(1).unsqueeze(1)
                        return row.to_broadcast([P, NH, 2, HALF])
                    dve.drain()
                    dve.tensor_tensor(rot_c[:, :, :, :], rot, spread(cosb[:, bass.ds(b * NT + t, 1), :]), ALU.mult)
                    dve.tensor_tensor(rot_s[:, :, :, :], rot, spread(sinb[:, bass.ds(b * NT + t, 1), :]), ALU.mult)
                elif step == 4:
                    dve.drain()
                    dve.tensor_tensor(rot[:, :, 0], rot_c[:, :, 0], rot_s[:, :, 1], ALU.subtract)
                    dve.tensor_tensor(rot[:, :, 1], rot_c[:, :, 1], rot_s[:, :, 0], ALU.add)
                else:
                    dve.drain()
                    dve.tensor_copy(kdup[:, :, :, :], q3[:, HEADS:NH].unsqueeze(2).to_broadcast([P, KV_HEADS, 2, HEAD_DIM])
                                    ).then_inc(qk_ready.sem, 1)

            with dve.Fori(0, NB) as b:
                for c in range(DNT):
                    split(b, U_DN + c + 2)
                    if c == 0:
                        dve.wait_ge(stored.sem, stored.at(b, 0))
                        dve.tensor_copy(qkv[:, :, 0:HALO], halo[:, :, :])
                        dve.drain()
                    dve.wait_ge(a_evac.sem, a_evac.at(b, J_DN + c + 1))
                    dve.wait_ge(silu_done.sem, silu_done.at(b, c - 1))
                    dve.tensor_copy(halo[:, c, :], qkv[:, c, BLK:BLK + HALO])
                    a = acc[c % 2][:, :]
                    dve.tensor_scalar(a, qkv[:, c, 0:BLK], taps[:, c, 0:1], None, ALU.mult)
                    for k in range(1, TAPS):
                        dve.drain()
                        last = dve.scalar_tensor_tensor(a, qkv[:, c, k:k + BLK], taps[:, c, k:k + 1], a, ALU.mult, ALU.add)
                    last.then_inc(conv_done.sem, 1)
                for u in range(U_AT, U_GATE):
                    split(b, u + 2)
                    if u == U_BA:
                        for step in range(6):
                            prepare(b, 0, step)
                ba = mb[:, 0:NT * 8].rearrange("p (t n) -> p t n", t=NT)
                dve.wait_ge(ba_turned.sem, ba_turned.at(b, 1))
                dve.tensor_tensor(g_a[:, :, :], ba[:, :, 4:8], dtb[:, :].unsqueeze(1).to_broadcast(TH), ALU.add
                                  ).then_inc(g_add.sem, 1)
                dve.wait_ge(g_exp.sem, g_exp.at(b, 1))
                dve.tensor_scalar(g_e[:, :, :], g_e[:, :, :], 1.0, None, ALU.add)
                dve.drain()
                dve.reciprocal(g_b[:, :, :], g_e[:, :, :])
                dve.drain()
                dve.tensor_scalar(g_nb[:, :, :], g_b[:, :, :], -1.0, None, ALU.mult)
                dve.wait_ge(g_abs.sem, g_abs.at(b, 1))
                dve.tensor_scalar(g_y[:, :, :], g_c[:, :, :], 1.0, None, ALU.add).then_inc(g_y1.sem, 1)
                dve.drain()
                dve.tensor_scalar(g_r[:, :, :], g_y[:, :, :], -1.0, None, ALU.add)
                dve.reciprocal(g_e[:, :, :], g_y[:, :, :])
                dve.tensor_scalar(g_a[:, :, :], g_a[:, :, :], 0.0, None, ALU.max)
                dve.drain()
                dve.tensor_tensor(g_c[:, :, :], g_c[:, :, :], g_r[:, :, :], ALU.subtract)
                dve.drain()
                dve.tensor_tensor(g_c[:, :, :], g_c[:, :, :], g_e[:, :, :], ALU.mult)
                dve.drain()
                dve.wait_ge(g_ln.sem, g_ln.at(b, 1))
                dve.tensor_tensor(g_c[:, :, :], g_c[:, :, :], g_l[:, :, :], ALU.add)
                dve.drain()
                dve.tensor_tensor(g_c[:, :, :], g_c[:, :, :], g_a[:, :, :], ALU.add)
                dve.drain()
                dve.tensor_tensor(g_g[:, :, :], g_c[:, :, :], nea[:, :].unsqueeze(1).to_broadcast(TH), ALU.mult
                                  ).then_inc(g_ready.sem, 1)
                dve.wait_ge(g_cp.sem, g_cp.at(b, 1))
                dve.tensor_tensor(g_r[:, :, :], gcs[:, 1], gcs[:, 0], ALU.subtract).then_inc(g_diff.sem, 1)
                dve.wait_ge(g_all.sem, g_all.at(b, 1))
                dve.tensor_tensor(g_nbe[:, :, :], g_nb[:, :, :], g_egc[:, :, :], ALU.mult).then_inc(g_nbe_ready.sem, 1)

                for t in range(NT):
                    dve.tensor_copy(sc[:, :, P:P + 1], snk[:, :].unsqueeze(2))
                    for g in range(2):
                        wait_alone(dve, own_copied, own_copied.at(b, 2 * t + g + 1))
                        before = halves(g, 1)
                        if t == 0:
                            if g:
                                dve.drain()
                            dve.tensor_scalar(by_parity(prev_sc[:, :, :]), before, neg_first[:, 0:1], None, ALU.add)
                            dve.drain()
                            before = by_parity(prev_sc[:, :, :])
                        dve.copy_predicated(out=by_parity(sc[:, 4 * g:4 * g + 4, 0:P]),
                                            mask=m_prev[:, :].unsqueeze(1).unsqueeze(1).to_broadcast([P, 2, 2, P]),
                                            data=before)
                    dve.drain()
                    dve.tensor_reduce(a_mx[:, :], sc[:, :, :], AX.X, ALU.max)
                    dve.drain()
                    dve.tensor_scalar(a_mx[:, :], a_mx[:, :], -1.0, None, ALU.mult).then_inc(maxed.sem, 1)
                    split(b, U_GATE + 4 * t + 2)
                    dve.wait_ge(exped.sem, exped.at(b, t + 1))
                    dve.reciprocal(a_sm[:, :], a_sm[:, :])
                    dve.drain()
                    dve.tensor_tensor(ps_[:, :, 0:P], ps_[:, :, 0:P], over_heads(a_sm[:, :], HEADS), ALU.mult
                                      ).then_inc(probs_ready.sem, 1)
                    for g in range(2):
                        dve.wait_ge(probs_turned.sem, probs_turned.at(b, 2 * t + g + 1))
                        src = m(2 - 2 * g)
                        dve.tensor_tensor(pT[g][0][:, :, :], src, each_head(tri[:, :]), ALU.mult)
                        dve.tensor_tensor(pT[g][1][:, :, :], src, each_head(gtm[:, :]), ALU.mult
                                          ).then_inc(probsT_ready.sem, 1)
                    dve.wait_ge(d_sq.sem, d_sq.at(b, t + 1))
                    dve.tensor_reduce(d_ss[:, :], t_sq[:, :, :], AX.X, ALU.add)
                    dve.drain()
                    dve.tensor_scalar(d_ss[:, :], d_ss[:, :], EPS, None, ALU.add).then_inc(d_ssq.sem, 1)
                    dve.tensor_tensor(t_vb[:, :, :], m(2), over_heads(g_b[:, t, :]), ALU.mult)
                    dve.wait_ge(d_rstd.sem, d_rstd.at(b, t + 1))
                    dve.tensor_scalar(d_rq[:, :], d_rs[:, 0:4], DN_DIM ** -0.5, None, ALU.mult)
                    dve.drain()
                    dve.tensor_tensor(d_qs[:, :], d_rq[:, :], g_egc[:, t, :], ALU.mult)
                    dve.drain()
                    dve.tensor_tensor(t_q[:, :, :], m(0), over_heads(d_qs[:, :]), ALU.mult)
                    dve.tensor_tensor(t_kn[:, :, :], m(1), over_heads(d_rs[:, 4:8]), ALU.mult).then_inc(kn_ready.sem, 1)
                    split(b, U_GATE + 4 * t + 3)
                    dve.wait_ge(kn_turned.sem, kn_turned.at(b, t + 1))
                    for h in range(DN_HEADS):
                        last = dve.tensor_scalar(t_dec[:, h, :], m(2)[:, h, :], gcs[:, 0, t, h:h + 1], 0.0,
                                                 ALU.subtract, ALU.max)
                    last.then_inc(clipped.sem, 1)
                    dve.wait_ge(gram.sem, gram.at(b, t + 1))
                    dve.wait_ge(decays.sem, decays.at(b, t + 1))
                    for h in range(DN_HEADS):
                        dve.scalar_tensor_tensor(t_N[:, h, :], m(0)[:, h, :], g_nb[:, t, h:h + 1], t_dec[:, h, :],
                                                 ALU.mult, ALU.mult)
                    for h in range(DN_HEADS):
                        last = dve.scalar_tensor_tensor(t_A[:, h, :], m(1)[:, h, :], d_rq[:, h:h + 1], t_dec[:, h, :],
                                                        ALU.mult, ALU.mult)
                    last.then_inc(na_ready.sem, 1)
                    for h in range(DN_HEADS):
                        dve.scalar_tensor_tensor(t_R[:, h, :], m(3)[:, h, :], g_nbe[:, t, h:h + 1], t_vb[:, h, :],
                                                 ALU.mult, ALU.add)
                    split(b, U_GATE + 4 * t + 4)
                    wait_alone(dve, nT_ready, nT_ready.at(b, t + 1))
                    dve.copy_predicated(out=t_T[:, :, :], mask=each_head(mT[0][:, :]), data=t_N[:, :, :]
                                        ).then_inc(t_merged.sem, 1)
                    dve.copy_predicated(out=t_U[:, :, :], mask=each_head(mU[0][:, :]), data=m(2)).then_inc(u_merged.sem, 1)
                    dve.tensor_tensor(t_AT[:, :, :], m(0), each_head(tri[:, :]), ALU.mult)
                    for i in range(len(LEVELS)):
                        if i < len(LEVELS) - 1:
                            wait_alone(dve, t_prod, t_prod.at(b, t * (len(LEVELS) - 1) + i + 1))
                            dve.copy_predicated(out=t_T[:, :, :], mask=each_head(mT[i + 1][:, :]), data=m(3)
                                                ).then_inc(t_merged.sem, 1)
                        wait_alone(dve, u_prod, u_prod.at(b, t * len(LEVELS) + i + 1))
                        dve.copy_predicated(out=t_U[:, :, :], mask=each_head(mU[i + 1][:, :]), data=m(2)
                                            ).then_inc(u_merged.sem, 1)
                        if t < NT - 1:
                            prepare(b, t + 1, i)
                        if i == 1 and t == NT - 1:
                            dve.wait_ge(oT_high.sem, oT_high.at(b, 1))
                            dve.tensor_tensor(oT_lo[:, 0:4, :], oT[:, 0:4, :], oT_hi[:, 0:4, :].bitcast(fp32), ALU.subtract
                                              ).then_inc(oT_ready.sem, 1)
                    split(b, U_GATE + 4 * t + 5)
                    dve.wait_ge(kv_prod.sem, kv_prod.at(b, t + 1))
                    for h in range(DN_HEADS):
                        last = dve.scalar_tensor_tensor(state[:, h, :], state[:, h, :], g_dl[:, t, h:h + 1], m(3)[:, h, :],
                                                        ALU.mult, ALU.add)
                    last.then_inc(s_ready.sem, 1)
                    dve.wait_ge(o_sq.sem, o_sq.at(b, t + 1))
                    dve.tensor_reduce(o_ss[:, :], t_T[:, :, :], AX.X, ALU.add)
                    dve.drain()
                    dve.tensor_scalar(o_ss[:, :], o_ss[:, :], 1.0 / DN_DIM, EPS, ALU.mult, ALU.add).then_inc(o_ssq.sem, 1)
                    dve.wait_ge(o_rstd.sem, o_rstd.at(b, t + 1))
                    for h in range(DN_HEADS):
                        last = dve.scalar_tensor_tensor(t_o[:, h, :], m(0)[:, h, :], o_rs[:, h:h + 1],
                                                        z_act[:, t, h * P:h * P + P], ALU.mult, ALU.mult)
                    last.then_inc(o_ready.sem, 1)
                dve.memset(neg_first[:, :], 0.0)
                dve.wait_ge(oT_high.sem, oT_high.at(b, 2))
                dve.tensor_tensor(oT_lo[:, 4:8, :], oT[:, 4:8, :], oT_hi[:, 4:8, :].bitcast(fp32), ALU.subtract
                                  ).then_inc(oT_ready.sem, 1)
                for i in range(KD + 1):
                    if i < KD:
                        split(b, U_BRANCH + i + 2)
                        j = J_BRANCH + 2 * i
                        dve.drain()
                        dve.wait_ge(full.sem, full.at(b, j + 2))
                        dve.wait_ge(gate_open.sem, gate_open.at(b, i + 1))
                        dve.tensor_tensor(br_a[:, :], bank(j), gates[:, 2 * i, :], ALU.mult)
                        dve.tensor_tensor(br_d[:, :], bank(j + 1), gates[:, 2 * i + 1, :], ALU.mult).then_inc(v_evac.sem, 2)
                        dve.drain()
                        dve.tensor_tensor(br_m[i % 2][:, :], br_a[:, :], br_d[:, :], ALU.add).then_inc(mg_full.sem, 1)
                    if i:
                        dve.wait_ge(mg_high.sem, mg_high.at(b, i))
                        dve.tensor_tensor(mg_lo[:, i - 1, :], br_m[(i - 1) % 2][:, :], mg_hi[:, i - 1, :].bitcast(fp32),
                                          ALU.subtract).then_inc(mg_ready.sem, 1)

                def add_columns(j, c, row, done=None):
                    part = slice(c * 256, c * 256 + 256)
                    dve.wait_ge(full.sem, full.at(b, j + 2))
                    dve.tensor_tensor(scaled[:, :, :], pair(j), gate_row[:, row, part].unsqueeze(1).to_broadcast([P, NT, 256]),
                                      ALU.mult).then_inc(v_evac.sem, 2)
                    dve.drain()
                    last = dve.tensor_tensor(x1[:, :, part], x1[:, :, part], scaled[:, :, :], ALU.add)
                    if done is not None:
                        last.then_inc(done.sem, 1)
                    dve.drain()

                for c in range(4):
                    split(b, U_OUT + 2 * c + 2)
                    split(b, U_OUT + 2 * c + 3)
                    if c == 0:
                        dve.wait_ge(x1_loaded.sem, x1_loaded.at(b, 16))
                    add_columns(J_OUT + 2 * c, c, 0, x1_out if c == 3 else None)
                for i in range(NT + 2):
                    if i < NT:
                        norm_mean(i, n_sq.at(b, i + 1))
                    if 1 <= i <= NT:
                        ps = mb[:, ((i - 1) % 2) * 1024:((i - 1) % 2) * 1024 + 1024].rearrange("p (k n) -> p k n", k=KD)
                        dve.drain()
                        dve.wait_ge(n_turn.sem, n_turn.at(b, i))
                        dve.tensor_tensor(nf[:, (i - 1) % 2, :].rearrange("p (k n) -> p k n", k=KD), ps,
                                          mod_a[:, 1, :].unsqueeze(2).to_broadcast([P, KD, P]), ALU.mult
                                          ).then_inc(n_scaled.sem, 1)
                    if i >= 2:
                        norm_low(i - 2, n_high.at(b, i - 1), h2_hi, h2_lo)
                n1 = 0
                for gi, (u0, j0, f0, count) in enumerate(places):
                    for f in range(count + 1):
                        if f < count:
                            split(b, u0 + 2 * f + 2)
                            split(b, u0 + 2 * f + 3)
                            dve.drain()
                            dve.wait_ge(full.sem, full.at(b, j0 + 2 * f + 2))
                            dve.wait_ge(a_evac.sem, a_evac.at(b, WHO[:j0 + 2 * f + 1].count("A")))
                            dve.tensor_tensor(hf[f % 2][:, :], bank(j0 + 2 * f + 1), hs[f % 2][:, :], ALU.mult
                                              ).then_inc(v_evac.sem, 1)
                        if f:
                            dve.wait_ge(hid_high.sem, hid_high.at(b, f0 + f))
                            dve.tensor_tensor(hid_lo[:, f - 1, :], hf[(f - 1) % 2][:, :], hid_hi[:, f - 1, :].bitcast(fp32),
                                              ALU.subtract).then_inc(hid_ready.sem, 1)
                        if gi < 2 and f in (2, 6):
                            norm_mean(n1, n_sq.at(b, 4 + n1 + 1))
                            norm_rows(n1, n_pow.at(b, 4 + n1 + 1), xs[:, n1 % 2, :], xs[:, n1 % 2, :])
                        if gi < 2 and f in (3, 7):
                            norm_modulate(n1, n_turn.at(b, 4 + n1 + 1), 0)
                        if gi < 2 and f in (4, 8):
                            norm_low(n1, n_high.at(b, 4 + n1 + 1), h_hi, h_lo)
                            n1 += 1
                    for c in range(4):
                        split(b, u0 + 2 * count + 2 * c + 2)
                        split(b, u0 + 2 * count + 2 * c + 3)
                        add_columns(j0 + 2 * count + 2 * c, c, 1, x1_done if gi == 2 else None)

        @block.tensor
        def _(pe):
            pe.wait_ge(pool_set, 1)
            for c in range(12):
                v, half = divmod(c, 2)
                pe.wait_ge(ada_done, c + 1)
                if c >= 2:
                    pe.wait_ge(ada_read, c - 1)
                ps = mb[:, (c % 2) * 512:(c % 2) * 512 + 512]
                if v in (2, 5):
                    last = pe.matmul(ps, ones[:, :], ada_sum[:, c % 2, :], start=True, stop=True)
                else:
                    for k in range(4):
                        last = pe.matmul(ps[:, k:k + 1], ada_sum[:, c % 2, k * P:k * P + P], ones[:, 0:1],
                                         start=True, stop=True)
                last.then_inc(ada_prod, 1)

            def norm_turn(n, value):
                pe.wait_ge(n_xn.sem, value)
                for k in range(KD):
                    last = pe.transpose(mb[:, (n % 2) * 1024 + k * P:(n % 2) * 1024 + k * P + P],
                                        xs[:, n % 2, k * P:k * P + P], ident[:, :])
                last.then_inc(n_turn.sem, 1)

            pe.wait_ge(ada_read, 12)
            for t in range(NT):
                norm_turn(t, t + 1)

            def free_bank(b, j):
                k = j - 4
                who = WHO[k % J_PER]
                s, per = (a_evac, A_PER) if who == "A" else (v_evac, V_PER)
                n = WHO[:k + 1].count(who) if k >= 0 else WHO[:k % J_PER + 1].count(who) - per
                pe.wait_ge(s.sem, s.at(b, n))

            def by_feature(b, u, j, hi, lo, kk=range(KD), first=0, count=None):
                s, n = u % RING, 3 * len(kk)
                count = n if count is None else count
                if first == 0:
                    pe.wait_ge(w_ready.sem, w_ready.at(b, u + 1))
                    free_bank(b, j)
                for i in range(first, first + count):
                    k, part = kk[i // 3], i % 3
                    w = (w_lo if part == 2 else w_hi)[s][:, k * P:k * P + P]
                    r = (lo if part == 1 else hi)[:, k, :]
                    last = pe.matmul(bank(j), w, r, start=(i == 0), stop=(i == n - 1))
                return last

            def by_token(b, u, j, half, hi, lo, kn=4):
                s = u % RING
                pe.wait_ge(w_ready.sem, w_ready.at(b, u + 1))
                if half == 0:
                    free_bank(b, j)
                    free_bank(b, j + 1)
                for t in range(NT):
                    for k in range(kn):
                        for part in range(3):
                            l = (lo if part == 1 else hi)[:, half * kn + k, t * P:t * P + P]
                            w = (w_lo if part == 2 else w_hi)[s][:, k * 256:k * 256 + 256]
                            first = half == 0 and k == 0 and part == 0 and t % 2 == 0
                            final = half == 1 and k == kn - 1 and part == 2
                            last = pe.matmul(pair(j)[:, t, :], l, w, start=first, stop=final, skip_group_check=True)
                return last

            def turn_qk(b, t):
                pe.wait_ge(qk_ready.sem, qk_ready.at(b, t + 1))
                for h in range(4):
                    pe.transpose(m(2)[:, h, :], qk[:, h * P:h * P + P], ident[:, :])
                for g in range(2):
                    last = pe.transpose(m(3, 2)[:, g, :], kdup[:, g].rearrange("p a d -> p (a d)"), ident[:, :])
                last.then_inc(qk_turned.sem, 1)

            with pe.Fori(0, NB) as b:

                def token_chunk(u, j, hi, lo, kn=4, ready=None):
                    for half in range(2):
                        if ready is not None:
                            ready(half)
                        last = by_token(b, u + half, j, half, hi, lo, kn)
                        if half == 0:
                            last.then_inc(half_done.sem, 1)
                    last.then_inc(full.sem, 2)

                def feature_unit(u, j, hi, lo, steps=1):
                    by_feature(b, u, j, hi, lo).then_inc(full.sem, steps)

                pe.wait_ge(n_ready.sem, n_ready.at(b, 0))
                for c in range(DNT):
                    feature_unit(U_DN + c, J_DN + c, h_hi, h_lo)
                for c in range(3):
                    token_chunk(U_AT + 2 * c, J_AT + 2 * c, h_hi, h_lo)
                feature_unit(U_BA, J_BA, h_hi, h_lo, steps=2)
                token_chunk(U_Z, J_Z, h_hi, h_lo)
                pe.wait_ge(n_full.sem, n_full.at(b, 0))
                wait_alone(pe, a_evac, a_evac.at(b, WHO[:J_BA + 2].count("A")))
                for t in range(NT):
                    last = pe.transpose(mb[:, t * 8:t * 8 + 8], ba_sb[:, t * P:t * P + P], ident[0:8, 0:8])
                last.then_inc(ba_turned.sem, 1)
                token_chunk(U_Z + 2, J_Z + 2, h_hi, h_lo)
                turn_qk(b, 0)
                pe.wait_ge(g_ready.sem, g_ready.at(b, 1))
                g2d = g_g[:, :, :].rearrange("p t h -> p (t h)")
                pe.matmul(mb[:, 512:528], tri[:, :], g2d, start=True, stop=True)
                pe.matmul(mb[:, 528:544], ones[:, :], g2d, start=True, stop=True).then_inc(g_sums.sem, 1)

                for t in range(NT):
                    cols = slice(t * P, t * P + P)
                    left = [0]

                    def fill(count):
                        count = min(count, 4 * 24 - left[0])
                        while count:
                            i, at_ = divmod(left[0], 24)
                            n = min(count, 24 - at_)
                            u, j = U_GATE + 4 * t + i, J_GATE + 4 * t + i
                            last = by_feature(b, u, j, h_hi, h_lo, first=at_, count=n)
                            if at_ + n == 24:
                                last.then_inc(full.sem, 1)
                            left[0] += n
                            count -= n

                    fill(6)
                    pe.wait_ge(qT_ready.sem, qT_ready.at(b, t + 1))
                    if t:
                        pe.wait_ge(dn_saved.sem, dn_saved.at(b, t))
                    else:
                        pe.wait_ge(g_nbe_ready.sem, g_nbe_ready.at(b, 1))
                    for g in range(2):
                        for parity in range(2):
                            rows = slice(64 * parity, 64 * parity + 64)
                            for old, keys in enumerate((kT[t % 2], kT[(t + 1) % 2])):
                                for a in range(2):
                                    last = pe.matmul(m(2 * g + parity)[:, 2 * old + a, :], qT[rows, 2 * g + a, :],
                                                     keys[rows, g, :], start=True, stop=True)
                        last.then_inc(scores.sem, 1)
                        fill(4)
                    fill(16)
                    pe.wait_ge(probs_ready.sem, probs_ready.at(b, t + 1))
                    for g in range(2):
                        for h in range(4):
                            last = pe.transpose(m(2 - 2 * g)[:, h, :], ps_[:, 4 * g + h, 0:P], ident[:, :])
                        last.then_inc(probs_turned.sem, 1)
                    for g in range(2):
                        pe.wait_ge(probsT_ready.sem, probsT_ready.at(b, 2 * t + g + 1))
                        v_own = proj[:, t, QKW + 64 * g:QKW + 64 * g + 64]
                        v_old = (proj[:, t - 1, QKW + 64 * g:QKW + 64 * g + 64] if t
                                 else v_prev[:, 64 * g:64 * g + 64])
                        for odd in range(2):
                            o_ap = m(3)[64 * odd:64 * odd + 64, 2 * g:2 * g + 2, :]
                            pe.matmul(o_ap, v_own, pT[g][0][:, odd::2, :], start=True, stop=False)
                            last = pe.matmul(o_ap, v_old, pT[g][1][:, odd::2, :], start=False, stop=True)
                    last.then_inc(attn_out.sem, 1)
                    if t == 0:
                        pe.wait_ge(silu_done.sem, silu_done.at(b, DNT))
                    for i in range(3):
                        for h in range(4):
                            last = pe.transpose(m(i)[:, h, :], qkv[:, 4 * i + h, HALO + t * P:HALO + t * P + P], ident[:, :])
                    last.then_inc(tok_turned.sem, 1)
                    fill(18)
                    pe.wait_ge(kn_ready.sem, kn_ready.at(b, t + 1))
                    pe.wait_ge(attn_saved.sem, attn_saved.at(b, t + 1))
                    for h in range(4):
                        pe.transpose(m(3)[:, h, :], t_kn[:, h, :], ident[:, :])
                    for h in range(4):
                        pe.transpose(m(0)[:, h, :], t_q[:, h, :], ident[:, :])
                    for h in range(4):
                        last = pe.matmul(m(2)[:, h, :], g_g[:, t, h:h + 1].to_broadcast([P, P]), tri[:, :],
                                         start=True, stop=True)
                    last.then_inc(kn_turned.sem, 1)
                    fill(6)
                    pe.wait_ge(knT_ready.sem, knT_ready.at(b, t + 1))
                    pe.wait_ge(s_ready.sem, s_ready.at(b, t))
                    for h in range(4):
                        pe.matmul(m(0)[:, h, :], t_knT[:, h, :], t_knT[:, h, :], start=True, stop=True)
                    for h in range(4):
                        pe.matmul(m(1)[:, h, :], qkv[:, h, HALO + t * P:HALO + t * P + P], t_knT[:, h, :],
                                  start=True, stop=True)
                    for h in range(4):
                        last = pe.matmul(m(3)[:, h, :], t_knT[:, h, :], state[:, h, :], start=True, stop=True)
                    last.then_inc(gram.sem, 1)
                    fill(8)
                    pe.wait_ge(na_ready.sem, na_ready.at(b, t + 1))
                    for h in range(4):
                        pe.transpose(m(2)[:, h, :], t_N[:, h, :], ident[:, :])
                    for h in range(4):
                        last = pe.transpose(m(0)[:, h, :], t_A[:, h, :], ident[:, :])
                    last.then_inc(na_turned.sem, 1)
                    fill(2)
                    pe.wait_ge(nT_ready.sem, nT_ready.at(b, t + 1))
                    for i in range(len(LEVELS)):
                        pe.wait_ge(t_merged.sem, t_merged.at(b, t * len(LEVELS) + i + 1))
                        for h in range(4):
                            last = pe.matmul(m(1)[:, h, :], t_NT[:, h, :], t_T[:, h, :], start=True, stop=True)
                        last.then_inc(nt_prod.sem, 1)
                        fill(1)
                        pe.wait_ge(x_ready.sem, x_ready.at(b, t * len(LEVELS) + i + 1))
                        pe.wait_ge(u_merged.sem, u_merged.at(b, t * (len(LEVELS) + 1) + i + 1))
                        if i < len(LEVELS) - 1:
                            for h in range(4):
                                last = pe.matmul(m(3)[:, h, :], t_U[:, h, :], t_X[:, h, :], start=True, stop=True)
                            last.then_inc(t_prod.sem, 1)
                        for h in range(4):
                            last = pe.matmul(m(2)[:, h, :], t_X[:, h, :], t_U[:, h, :], start=True, stop=True)
                        last.then_inc(u_prod.sem, 1)
                        fill(1)
                    pe.wait_ge(u_merged.sem, u_merged.at(b, (t + 1) * (len(LEVELS) + 1)))
                    for h in range(4):
                        last = pe.matmul(m(1)[:, h, :], t_U[:, h, :], t_R[:, h, :], start=True, stop=True)
                    last.then_inc(vn_prod.sem, 1)
                    fill(3)
                    pe.wait_ge(vn_ready.sem, vn_ready.at(b, t + 1))
                    for h in range(4):
                        pe.matmul(m(0)[:, h, :], t_qT[:, h, :], state[:, h, :], start=True, stop=False)
                        last = pe.matmul(m(0)[:, h, :], t_AT[:, h, :], t_vn[:, h, :], start=False, stop=True)
                    last.then_inc(o_prod.sem, 1)
                    pe.wait_ge(kdec_ready.sem, kdec_ready.at(b, t + 1))
                    for h in range(4):
                        last = pe.matmul(m(3)[:, h, :], t_kdec[:, h, :], t_vn[:, h, :], start=True, stop=True)
                    last.then_inc(kv_prod.sem, 1)
                    fill(8)
                    if t < NT - 1:
                        pe.wait_ge(s_ready.sem, s_ready.at(b, t + 1))
                        turn_qk(b, t + 1)
                    fill(4 * 24)
                    pe.wait_ge(o_ready.sem, o_ready.at(b, t + 1))
                    for h in range(4):
                        last = pe.transpose(m(1)[:, h, :], t_o[:, h, :], ident[:, :])
                    last.then_inc(o_turned.sem, 1)

                for i in range(KD):
                    u, j = U_BRANCH + i, J_BRANCH + 2 * i
                    pe.wait_ge(w_ready.sem, w_ready.at(b, u + 1))
                    for side in range(2):
                        if i == 0:
                            pe.wait_ge(oT_ready.sem, oT_ready.at(b, side + 1))
                        free_bank(b, j + side)
                        s = u % RING
                        for k in range(4):
                            for part in range(3):
                                kk = 4 * side + k
                                w = (w_lo if part == 2 else w_hi)[s][:, kk * P:kk * P + P]
                                r = (oT_lo if part == 1 else oT_hi)[:, kk, :]
                                last = pe.matmul(bank(j + side), w, r, start=(k == 0 and part == 0),
                                                 stop=(k == 3 and part == 2))
                        last.then_inc(full.sem, 1)
                for c in range(4):
                    token_chunk(U_OUT + 2 * c, J_OUT + 2 * c, mg_hi, mg_lo,
                                ready=(lambda half: pe.wait_ge(mg_ready.sem, mg_ready.at(b, 4 * half + 4))) if c == 0 else None)
                for i in range(NT):
                    if i >= 2:
                        pe.wait_ge(n_scaled.sem, n_scaled.at(b, i - 1))
                    norm_turn(i, n_xn.at(b, i + 1))
                pe.wait_ge(n_ready.sem, n_ready.at(b, NT))
                n1 = 0
                for gi, (u0, j0, f0, count) in enumerate(places):
                    for f in range(count):
                        feature_unit(u0 + 2 * f, j0 + 2 * f, h2_hi, h2_lo)
                        if gi < 2 and f in (3, 7):
                            norm_turn(n1, n_xn.at(b, 4 + n1 + 1))
                            n1 += 1
                        feature_unit(u0 + 2 * f + 1, j0 + 2 * f + 1, h2_hi, h2_lo)
                    for c in range(4):
                        kn = count // 2
                        token_chunk(u0 + 2 * count + 2 * c, j0 + 2 * count + 2 * c, hid_hi, hid_lo, kn,
                                    ready=(lambda half: pe.wait_ge(hid_ready.sem, hid_ready.at(b, f0 + kn * (half + 1))))
                                    if c == 0 else None)


def kernel(x, c, positions, ada_w, ada_b, norm1_g, w_in, conv_w, q_norm_g, k_norm_g, sinks, a_log, dt_bias,
           dn_norm_g, w_branch, w_out, norm2_g, w_gate_up, w_down):
    import concourse.bacc as _bacc
    from concourse.bass_utils import run_bass_kernel_spmd as _run

    arr = np.ascontiguousarray
    f = lambda a: np.asarray(a)
    w_in_, wb, wo, wgu, wd = f(w_in)[0], f(w_branch)[0], f(w_out)[0], f(w_gate_up)[0], f(w_down)[0]

    def feature(w, n0):
        return w[:, n0:n0 + P].reshape(KD, P, P).transpose(1, 0, 2).reshape(P, UW)

    def token(w, r0, kn, n0):
        part = w[r0:r0 + kn * P, n0:n0 + 256].reshape(kn, P, 256).transpose(1, 0, 2).reshape(P, kn * 256)
        return np.pad(part, ((0, 0), (0, UW - kn * 256)))

    units = [feature(w_in_, C_DN + i * P) for i in range(DNT)]
    units += [token(w_in_, h * 512, 4, n * 256) for n in range(3) for h in range(2)]
    units += [feature(w_in_, C_BA)]
    units += [token(w_in_, h * 512, 4, C_Z + n * 256) for n in range(2) for h in range(2)]
    for i in range(KD):
        units += [feature(w_in_, C_GA + i * P), feature(w_in_, C_GD + i * P)]
    units += [feature(wb, i * P) for i in range(KD)]
    units += [token(wo, h * 512, 4, n * 256) for n in range(4) for h in range(2)]
    for first, count in FFN_GROUPS:
        for i in range(first, first + count):
            units += [feature(wgu, i * P), feature(wgu, FFN + i * P)]
        kn = count // 2
        units += [token(wd, (first + h * kn) * P, kn, n * 256) for n in range(4) for h in range(2)]
    assert len(units) == U_PER

    cols = lambda a: f(a).reshape(-1, P).T
    ada = f(ada_w)[0].reshape(KD, P, 12, 512).transpose(2, 1, 0, 3)
    ab = f(ada_b)[0].reshape(6, D)
    ins = {
        "x": f(x)[0],
        "cond": cols(c),
        "pos": f(positions)[0].reshape(SEQ // P, P).T,
        "ada_w": ada,
        "ada_bc": ab.reshape(6, KD, P).transpose(2, 0, 1),
        "ada_br": ab[[2, 5]].reshape(1, 2 * D),
        "g1": cols(norm1_g),
        "g2": cols(norm2_g),
        "qkg": np.broadcast_to(np.stack([f(q_norm_g)[0], f(k_norm_g)[0]])[None], (P, 2, HEAD_DIM)),
        "sinks": f(sinks),
        "a_log": f(a_log),
        "dt_bias": f(dt_bias),
        "conv_w": f(conv_w)[0].reshape(TAPS, DNT, P).transpose(2, 1, 0),
        "dn_g": f(dn_norm_g).reshape(P, 1),
        "wstream": np.stack(units),
    }
    nc = _bacc.Bacc("TRN2", target_bir_lowering=False, num_devices=1, dynamic_dma_scratch_size=1024)
    arrays, args = {}, []
    for name, a in ins.items():
        a = arr(a)
        arrays[f"in_{name}"] = a
        args.append(nc.dram_tensor(f"in_{name}", a.shape, mybir.dt.from_np(a.dtype), kind="ExternalInput").ap())
    args.append(nc.dram_tensor("out_0", (SEQ, D), mybir.dt.float32, kind="ExternalOutput").ap())
    layer_program(nc, *args)
    r = _run(nc, [arrays], core_ids=[0])
    return r.results[0]["out_0"].reshape(1, SEQ, D)
```
